# Optimizing a Trainium2 kernel written in Bass

```python
import math
import jax, jax.numpy as jnp
from jax import lax
import numpy as np

D_MODEL = 1024
BATCH = 1
SEQ = 256
DEPTH = 2
DEC_BATCH = 8
DEC_SEQ = 8
PAST_LEN = 2048
PAGE_SIZE = 128

GLA_HEADS = 4
GLA_DK = D_MODEL // 16
GLA_DV = D_MODEL // 8
GLA_LOWRANK = 16
GLA_TAU = 16.0
RET_HEADS = 4
RET_DK = D_MODEL // 16
RET_DV = D_MODEL // 8
ROPE_BASE = 10000.0
MIX_CHUNK = 32
XA_HEADS = 4
XA_DH = D_MODEL // 8
MEM_LEN = 256
D_FF = ((8 * D_MODEL // 3 + 255) // 256) * 256
CONV_W = 3
NORM_EPS = 1e-6
N_BRANCH = 3
SPLIT_SIZES = (GLA_HEADS * GLA_DK, GLA_HEADS * GLA_DK, GLA_HEADS * GLA_DV, GLA_HEADS * GLA_DV, GLA_LOWRANK,
               RET_HEADS * RET_DK, RET_HEADS * RET_DK, RET_HEADS * RET_DV, RET_HEADS * RET_DV,
               XA_HEADS * XA_DH, N_BRANCH * D_MODEL)
IN_COLS = sum(SPLIT_SIZES)

kernel_name = 'gla_retnet_memxattn_convffn_step'

def rms_norm(x, g, eps=NORM_EPS):
    xf = x.astype(jnp.float32)
    y = xf * lax.rsqrt(jnp.mean(xf * xf, axis=-1, keepdims=True) + eps)
    return (y * g.astype(jnp.float32)).astype(x.dtype)

def head_group_norm(x, g, eps=1e-5):
    xf = x.astype(jnp.float32)
    mu = jnp.mean(xf, axis=-1, keepdims=True)
    xc = xf - mu
    var = jnp.mean(xc * xc, axis=-1, keepdims=True)
    return (xc * lax.rsqrt(var + eps) * g.astype(jnp.float32)).astype(x.dtype)

def rope(x, pos):
    half = x.shape[-1] // 2
    inv = ROPE_BASE ** (-jnp.arange(half, dtype=jnp.float32) / half)
    ang = pos.astype(jnp.float32)[:, None] * inv[None, :]
    cos = jnp.cos(ang)[None, :, None, :]
    sin = jnp.sin(ang)[None, :, None, :]
    xf = x.astype(jnp.float32)
    x1, x2 = xf[..., :half], xf[..., half:]
    return jnp.concatenate([x1 * cos - x2 * sin, x1 * sin + x2 * cos], axis=-1).astype(x.dtype)

def chunked_gated_linear_attention(q, k, v, log_a, s0, chunk):
    B, L, H, K = q.shape
    V = v.shape[-1]
    n = L // chunk

    def blocks(t):
        return jnp.moveaxis(t.astype(jnp.float32).reshape(B, n, chunk, H, t.shape[-1]), 1, 0)

    causal = jnp.tril(jnp.ones((chunk, chunk), dtype=bool))

    def step(S, inp):
        qc, kc, vc, lc = inp
        b = jnp.cumsum(lc, axis=1)
        b_last = b[:, -1]
        q_dec = qc * jnp.exp(b)
        k_dec = kc * jnp.exp(-b)
        k_end = kc * jnp.exp(b_last[:, None] - b)
        scores = jnp.where(causal, jnp.einsum('bthk,bshk->bhts', q_dec, k_dec), 0.0)
        o = jnp.einsum('bthk,bhkv->bthv', q_dec, S) + jnp.einsum('bhts,bshv->bthv', scores, vc)
        S = jnp.exp(b_last)[..., None] * S + jnp.einsum('bshk,bshv->bhkv', k_end, vc)
        return S, o

    S, o = lax.scan(step, s0.astype(jnp.float32), (blocks(q), blocks(k), blocks(v), blocks(log_a)))
    o = jnp.moveaxis(o, 0, 1).reshape(B, L, H, V)
    return o.astype(v.dtype), S.astype(s0.dtype)

def memory_kv(mem, g, w_mem_kv):
    B, M, _ = mem.shape
    kv = rms_norm(mem, g) @ w_mem_kv
    k, v = jnp.split(kv, 2, axis=-1)
    return k.reshape(B, M, XA_HEADS, XA_DH), v.reshape(B, M, XA_HEADS, XA_DH)

def memory_attention(q, mem_k, mem_v):
    s = jnp.einsum('blhd,bmhd->bhlm', q, mem_k).astype(jnp.float32) * (XA_DH ** -0.5)
    p = jax.nn.softmax(s, axis=-1).astype(mem_v.dtype)
    return jnp.einsum('bhlm,bmhd->blhd', p, mem_v)

def layer(x, pos, s_gla, s_ret, conv_buf, mem_k, mem_v, p):
    B, L, D = x.shape
    chunk = math.gcd(L, MIX_CHUNK)
    h = rms_norm(x, p['norm1_g'])
    proj = h @ p['w_in']
    split_at = np.cumsum(SPLIT_SIZES)[:-1].tolist()
    gq, gk, gv, gr, ga, rq, rk, rv, rg, xq, gates = jnp.split(proj, split_at, axis=-1)

    log_a = jax.nn.log_sigmoid((ga @ p['gla_a_up'] + p['gla_a_b']).astype(jnp.float32)) / GLA_TAU
    o_gla, s_gla_new = chunked_gated_linear_attention(
        gq.reshape(B, L, GLA_HEADS, GLA_DK) * (GLA_DK ** -0.5),
        gk.reshape(B, L, GLA_HEADS, GLA_DK),
        gv.reshape(B, L, GLA_HEADS, GLA_DV),
        log_a.reshape(B, L, GLA_HEADS, GLA_DK), s_gla, chunk)
    o_gla = rms_norm(o_gla, p['gla_onorm_g'].reshape(GLA_HEADS, GLA_DV)).reshape(B, L, -1) * jax.nn.silu(gr)

    ret_log_decay = jnp.log(1.0 - 2.0 ** (-5.0 - jnp.arange(RET_HEADS, dtype=jnp.float32)))
    log_g = jnp.broadcast_to(ret_log_decay[None, None, :, None], (B, L, RET_HEADS, RET_DK))
    o_ret, s_ret_new = chunked_gated_linear_attention(
        rope(rq.reshape(B, L, RET_HEADS, RET_DK), pos),
        rope(rk.reshape(B, L, RET_HEADS, RET_DK), pos) * (RET_DK ** -0.5),
        rv.reshape(B, L, RET_HEADS, RET_DV), log_g, s_ret, chunk)
    o_ret = head_group_norm(o_ret, p['ret_gnorm_g'].reshape(RET_HEADS, RET_DV)).reshape(B, L, -1) * jax.nn.silu(rg)

    o_xa = memory_attention(xq.reshape(B, L, XA_HEADS, XA_DH), mem_k, mem_v).reshape(B, L, -1)

    gate = jax.nn.sigmoid((gates + p['b_gate']).astype(jnp.float32)).astype(x.dtype).reshape(B, L, N_BRANCH, D)
    merged = (gate[:, :, 0] * (o_gla @ p['w_br_gla'])
              + gate[:, :, 1] * (o_ret @ p['w_br_ret'])
              + gate[:, :, 2] * (o_xa @ p['w_br_xa']))
    x = x + merged @ p['w_out']

    h2 = rms_norm(x, p['norm2_g'])
    a, b = jnp.split(h2 @ p['w_up'], 2, axis=-1)
    a_seq = jnp.concatenate([conv_buf.astype(a.dtype), a], axis=1)
    conv_w = p['conv_w']
    c = p['conv_b'] + sum(a_seq[:, j:j + L] * conv_w[j] for j in range(CONV_W))
    x = x + (jax.nn.gelu(c) * b) @ p['w_down']
    new_buf = a_seq[:, a_seq.shape[1] - (CONV_W - 1):]
    return x, s_gla_new, s_ret_new, new_buf

def setup_inputs(seed: int = 0) -> dict:
    key = jax.random.key(seed)
    ks = jax.random.split(key, 32)
    f32 = jnp.float32

    def nrm(k, shape, scale):
        return jax.random.normal(k, shape, f32) * scale

    def gain(k, shape):
        return 1.0 + 0.02 * jax.random.normal(k, shape, f32)

    return {
        'x_prompt': nrm(ks[0], (BATCH, SEQ, D_MODEL), 1.0),
        'x_sample': nrm(ks[1], (DEC_BATCH, DEC_SEQ, D_MODEL), 1.0),
        'mem_prompt': nrm(ks[2], (BATCH, MEM_LEN, D_MODEL), 1.0),
        'state_gla': nrm(ks[3], (DEPTH, DEC_BATCH, GLA_HEADS, GLA_DK, GLA_DV), 1.0),
        'state_ret': nrm(ks[4], (DEPTH, DEC_BATCH, RET_HEADS, RET_DK, RET_DV), 1.0),
        'state_ffn_conv': nrm(ks[5], (DEPTH, DEC_BATCH, CONV_W - 1, D_FF), 1.0),
        'cache_mem_k': nrm(ks[6], (DEPTH, DEC_BATCH, MEM_LEN, XA_HEADS, XA_DH), 1.0),
        'cache_mem_v': nrm(ks[7], (DEPTH, DEC_BATCH, MEM_LEN, XA_HEADS, XA_DH), 1.0),
        'norm1_g': gain(ks[8], (DEPTH, D_MODEL)),
        'w_in': nrm(ks[9], (DEPTH, D_MODEL, IN_COLS), D_MODEL ** -0.5),
        'gla_a_up': nrm(ks[10], (DEPTH, GLA_LOWRANK, GLA_HEADS * GLA_DK), GLA_LOWRANK ** -0.5),
        'gla_a_b': nrm(ks[11], (DEPTH, GLA_HEADS * GLA_DK), 0.1),
        'gla_onorm_g': gain(ks[12], (DEPTH, GLA_HEADS * GLA_DV)),
        'ret_gnorm_g': gain(ks[13], (DEPTH, RET_HEADS * RET_DV)),
        'mem_norm_g': gain(ks[14], (DEPTH, D_MODEL)),
        'w_mem_kv': nrm(ks[15], (DEPTH, D_MODEL, 2 * XA_HEADS * XA_DH), D_MODEL ** -0.5),
        'w_br_gla': nrm(ks[16], (DEPTH, GLA_HEADS * GLA_DV, D_MODEL), (GLA_HEADS * GLA_DV) ** -0.5),
        'w_br_ret': nrm(ks[17], (DEPTH, RET_HEADS * RET_DV, D_MODEL), (RET_HEADS * RET_DV) ** -0.5),
        'w_br_xa': nrm(ks[18], (DEPTH, XA_HEADS * XA_DH, D_MODEL), (XA_HEADS * XA_DH) ** -0.5),
        'b_gate': nrm(ks[19], (DEPTH, N_BRANCH * D_MODEL), 0.02),
        'w_out': nrm(ks[20], (DEPTH, D_MODEL, D_MODEL), D_MODEL ** -0.5),
        'norm2_g': gain(ks[21], (DEPTH, D_MODEL)),
        'w_up': nrm(ks[22], (DEPTH, D_MODEL, 2 * D_FF), D_MODEL ** -0.5),
        'conv_w': nrm(ks[23], (DEPTH, CONV_W, D_FF), CONV_W ** -0.5),
        'conv_b': nrm(ks[24], (DEPTH, D_FF), 0.02),
        'w_down': nrm(ks[25], (DEPTH, D_FF, D_MODEL), D_FF ** -0.5),
        'final_g': gain(ks[26], (D_MODEL,)),
    }

def reference(x_prompt, x_sample, mem_prompt, state_gla, state_ret, state_ffn_conv, cache_mem_k, cache_mem_v,
              norm1_g, w_in, gla_a_up, gla_a_b, gla_onorm_g, ret_gnorm_g, mem_norm_g, w_mem_kv,
              w_br_gla, w_br_ret, w_br_xa, b_gate, w_out, norm2_g, w_up, conv_w, conv_b, w_down, final_g):
    Bp, Lp, _ = x_prompt.shape
    Ls = x_sample.shape[1]
    pos_p = jnp.arange(Lp, dtype=jnp.int32)
    pos_s = PAST_LEN + jnp.arange(Ls, dtype=jnp.int32)
    dt = x_prompt.dtype
    xp, xs = x_prompt, x_sample
    p_gla, p_ret, p_conv, p_mk, p_mv = [], [], [], [], []
    s_gla, s_ret, s_conv = [], [], []
    for i in range(DEPTH):
        p = {'norm1_g': norm1_g[i], 'w_in': w_in[i], 'gla_a_up': gla_a_up[i], 'gla_a_b': gla_a_b[i],
             'gla_onorm_g': gla_onorm_g[i], 'ret_gnorm_g': ret_gnorm_g[i], 'w_br_gla': w_br_gla[i],
             'w_br_ret': w_br_ret[i], 'w_br_xa': w_br_xa[i], 'b_gate': b_gate[i], 'w_out': w_out[i],
             'norm2_g': norm2_g[i], 'w_up': w_up[i], 'conv_w': conv_w[i], 'conv_b': conv_b[i], 'w_down': w_down[i]}
        mk, mv = memory_kv(mem_prompt, mem_norm_g[i], w_mem_kv[i])
        xp, g_new, r_new, c_new = layer(
            xp, pos_p,
            jnp.zeros((Bp, GLA_HEADS, GLA_DK, GLA_DV), dt),
            jnp.zeros((Bp, RET_HEADS, RET_DK, RET_DV), dt),
            jnp.zeros((Bp, CONV_W - 1, D_FF), dt), mk, mv, p)
        p_gla.append(g_new); p_ret.append(r_new); p_conv.append(c_new); p_mk.append(mk); p_mv.append(mv)
        xs, g_new, r_new, c_new = layer(
            xs, pos_s, state_gla[i], state_ret[i], state_ffn_conv[i], cache_mem_k[i], cache_mem_v[i], p)
        s_gla.append(g_new); s_ret.append(r_new); s_conv.append(c_new)
    y_prompt = rms_norm(xp, final_g)
    y_sample = rms_norm(xs, final_g)
    p_state_gla = jnp.stack(p_gla)
    p_state_ret = jnp.stack(p_ret)
    p_state_ffn_conv = jnp.stack(p_conv)
    p_cache_mem_k = jnp.stack(p_mk)
    p_cache_mem_v = jnp.stack(p_mv)
    s_state_gla = jnp.stack(s_gla)
    s_state_ret = jnp.stack(s_ret)
    s_state_ffn_conv = jnp.stack(s_conv)
    return (y_prompt, y_sample, p_state_gla, p_state_ret, p_state_ffn_conv, p_cache_mem_k, p_cache_mem_v,
            s_state_gla, s_state_ret, s_state_ffn_conv)


_drawn_inputs = setup_inputs


def setup_inputs(seed=0):
    import zlib

    import numpy as np

    out = dict(_drawn_inputs(seed))
    spreads = {}
    factors = {'gla_onorm_g': 5.651,
     'ret_gnorm_g': 5.49,
     'mem_norm_g': 7.74,
     'b_gate': 8.0,
     'conv_b': 3.616,
     'final_g': 7.77}
    for name, (base, spread) in spreads.items():
        noise = np.random.default_rng([zlib.crc32(name.encode()), seed]).standard_normal(out[name].shape)
        drawn = base * np.exp(spread * noise) if base else spread * noise
        out[name] = __import__('jax').numpy.asarray(drawn.astype(out[name].dtype))
    for name, factor in factors.items():
        out[name] = (out[name] * factor).astype(out[name].dtype)
    return out
```

```python
import math
from contextlib import ExitStack

import concourse.bass as bass
import numpy as np
from concourse import mybir

D_MODEL, SEQ, DEPTH, DEC_BATCH, DEC_SEQ, PAST = 1024, 256, 2, 8, 8, 2048
HEADS, DK, DV, LOWRANK, CHUNK, MEM = 4, 64, 128, 16, 32, 256
D_FF, CONV_W, ROPE_BASE = 2816, 3, 10000.0
P = 128
KT_ = D_MODEL // P
NS = DEC_BATCH * DEC_SEQ
T = SEQ + NS
NCH = SEQ // CHUNK
FT = D_FF // P
FA, FB = 12, 10
ARENA = 25728
UW = 8 * P
XSCALE = float(DV) ** -0.5

U_PAR, U_MK, U_MV, U_GA, U_XQ, U_QK, U_GV, U_RV, U_SIL, U_GATE = 0, 1, 5, 9, 10, 14, 22, 26, 30, 38
U_BR, U_OUT, U_UP1, U_DN1, U_UP2, U_DN2, UNITS = 62, 74, 82, 106, 118, 138, 148

C_N1, C_N2, C_MN, C_BG, C_CW, C_CB, C_AB, C_ON, C_GN, C_AU = 0, 8, 16, 24, 48, 114, 136, 138, 142, 146
C_CS = C_AU + 256
NPAR = C_CS + FT * 16
K_ID, K_ONE, K_CEN, K_PERM, K_MASK, K_COS, K_SIN = 0, 128, 256, 384, 512, 832, 1152
K_DQ, K_DK, K_RST, K_DE, K_BM, K_CM, NCON = 1472, 2112, 2752, 3072, 3076, 3084, 3088


def build_trunk(nc, w, x_in, mem_in, cache_k, cache_v, st_in, consts, final_g,
                y_out, pst_out, sst_out, conv_out, mk_out, mv_out):
    f32, f32r, u32 = mybir.dt.float32, mybir.dt.float32r, mybir.dt.uint32
    ALU, ACT, AX = mybir.AluOpType, mybir.ActivationFunctionType, mybir.AxisListType
    EPS, GEPS = 1e-6, 1e-5

    ctx = ExitStack()
    with ctx:
        def sb(name, shape, dt=f32):
            return ctx.enter_context(nc.sbuf_tensor(name, shape, dt))

        def sem(name):
            return ctx.enter_context(nc.semaphore(name))

        raw = sb("raw", [P, 4, UW])
        whi = sb("whi", [P, 4, UW], f32r)
        wlo = sb("wlo", [P, 2, UW], f32r)
        x = sb("x", [P, KT_, T])
        hh = sb("hh", [P, KT_, T], f32r)
        hl = sb("hl", [P, KT_, T], f32r)
        oh = sb("oh", [P, 12, T], f32r)
        ol = sb("ol", [P, 12, T], f32r)
        par = sb("par", [P, NPAR])
        con = sb("con", [P, NCON])
        fg = sb("fg", [P, KT_])
        rmem = sb("rmem", [P, MEM])
        rs = sb("rs", [P, T])
        cout = sb("cout", [P, FT, 18])
        sml = sb("sml", [P, 64])
        zp = sb("zp", [P, 2])
        zdec = sb("zdec", [P, 2, 8])
        qz = sb("qz", [P, 2, T])
        arena = sb("arena", [P, ARENA])

        free = [0]

        def ar(n):
            free[0] += n
            assert free[0] <= ARENA, free[0]
            return free[0] - n

        def at(o, *dims):
            n = math.prod(dims)
            v = arena[:, o:o + n]
            if len(dims) == 2:
                v = v.rearrange("p (a b) -> p a b", a=dims[0])
            if len(dims) == 3:
                v = v.rearrange("p (a b c) -> p a b c", a=dims[0], b=dims[1])
            return v

        o_qk = ar(8 * T)
        qd, kd = at(o_qk, 4, T), at(o_qk + 4 * T, 4, T)
        o_v = ar(6 * 512)
        vt = at(o_v, 2, 3, 512)
        memraw = at(o_v, KT_, MEM)
        o_sil = ar(8 * T)
        sil = at(o_sil, 8, T)
        o_ke = ar(4 * T)
        ke = at(o_ke, 4, T)
        o_kt = ar(4 * 3 * P)
        kT = at(o_kt, 4, 3, P)
        o_gn = ar(4 * T)
        o_g = ar(24 * T)
        G = at(o_g, 24, T)
        o_s = ar(4736 + 1024)
        S = at(o_s, NCH, P)
        s0 = at(o_s + 1024, 2, 8, P)
        kTm = at(o_s + 3072, 8, P)
        kTc = at(o_s + 4736, NCH, P)
        scm = at(o_s + 4096, 2 * T)
        memK, memV, xq = at(o_g, 4, MEM), at(o_g + 1024, 2, 512), at(o_g + 2048, 4, T)
        cache = at(o_g + 3328, 4, 1024)
        pp = at(o_g + 7424, 2, 2, MEM)
        pT = at(o_g + 8448, 2, 2, MEM)
        sS = at(o_g + 9472, 512)
        zsb, tmpa, ln1 = at(o_sil, 2, T), at(o_sil + 2 * T, 2, T), at(o_sil + 4 * T, 2, T)
        bcum, eb = at(o_sil + 6 * T, 2, T), at(o_gn, 2, T)
        enb, ee = at(o_sil + 2 * T, 2, T), at(o_sil + 4 * T, 2, T)
        rt = at(o_gn + 2 * T, 2, T)
        osb, gsq, gri, of_ = at(o_gn, 2 * T), at(o_gn + 2 * T, 2 * T), at(o_ke, 2 * T), at(o_ke + 2 * T, 2 * T)
        PART = (slice(0, 2 * SEQ), slice(2 * SEQ, 2 * T))
        TOK = (slice(0, SEQ), slice(SEQ, T))

        def heads(v):
            return v.rearrange("p (e t) -> p e t", e=2)
        sq, hf = at(o_gn, 2, T), at(o_qk, 8, T)
        acc, mt = at(o_ke, 2, T), at(o_kt, 2, T)
        mf = at(o_qk, 8, T)
        AP_ = 258 + 80
        apad = [at(o_g + i * 340, 340) for i in range(2)]
        cc = [[at(o_g + 700 + (3 * i + k) * 340, 340) for k in range(3)] for i in range(2)]
        gg = [at(o_g + 2800 + i * 340, 340) for i in range(2)]
        ff = at(o_g + 3500, 2, T)

        ident, ones, cent, perm = (con[:, k:k + P] for k in (K_ID, K_ONE, K_CEN, K_PERM))

        pb = [ctx.enter_context(nc.psum_tensor(f"bank{i}", [P, 512], f32)) for i in range(8)]
        A, C, B = pb[0:2], pb[2:4], pb[4:8]
        RB = [A[0], A[1], B[3]]

        loaded = [sem(f"unit_loaded{i}") for i in range(4)]
        hi_ready, lo_ready, unit_done = sem("hi_ready"), sem("lo_ready"), sem("unit_done")
        x_in_s, con_s, mem_s, fg_s = sem("x_loaded"), sem("consts_loaded"), sem("mem_loaded"), sem("final_g_loaded")
        cache_s = [sem(f"cache_loaded{i}") for i in range(4)]
        st_s = [sem(f"state_loaded{i}") for i in range(2)]
        out_s = {n: sem(f"stored_{n}") for n in ("mk", "mv", "pst", "sst0", "sst1", "conv", "y")}
        sq_ready, sq_used = sem("square_ready"), sem("square_summed")
        rs_ready, hf_ready, hh_ready, hl_ready = sem("rms_ready"), sem("normed_ready"), sem("normed_hi_ready"), sem("normed_lo_ready")
        mf_ready, mh_ready, ml_ready = sem("mem_normed"), sem("mem_hi_ready"), sem("mem_lo_ready")
        evac = sem("scalar_evacuated")
        memv_ready = sem("memv_ready")
        xscore, xmax, xexp, xp_ready = sem("xscores_done"), sem("xmax_ready"), sem("xexp_ready"), sem("xprobs_ready")
        xpt, xpt_ready, xo_done, xoh, xol = sem("xprobs_turned"), sem("xprobsT_ready"), sem("xout_done"), sem("xout_hi"), sem("xout_lo")
        xk_used, xv_used, xst = sem("cache_k_used"), sem("cache_v_used"), sem("sample_scoresT_ready")
        z_done, ln_ready, b_ready, eb_ready = sem("z_done"), sem("ln_ready"), sem("cumsum_ready"), sem("decays_ready")
        rot_done, rot_used, ke_ready, qd_ready = sem("rot_done"), sem("rot_used"), sem("kend_ready"), sem("qdkd_ready")
        v_ready, kt_done, kt_ready, ktm_ready, ktc_ready = (sem(n) for n in ("v_ready", "kendT_done", "kendT_ready", "kendT_of_batches", "kendT_of_chunks"))
        up_done, sc_done, scm_ready, s_ready = sem("chunk_updates_done"), sem("scores_done"), sem("scores_masked"), sem("states_ready")
        o_done, us_done, snew = sem("o_done"), sem("sample_updates_done"), sem("sample_states_new")
        osb_ready, xc_done, gsq_ready, gss_done, gsr_ready = sem("o_copied"), sem("o_centred"), sem("o_squared"), sem("o_square_summed"), sem("o_rms_ready")
        of_ready, ohr, olr = sem("o_final"), sem("o_hi_ready"), sem("o_lo_ready")
        sig_ready, sil_ready = sem("sigmoid_ready"), sem("silu_ready")
        br_used, mg_ready, mgh, mgl = sem("branch_products_used"), sem("merged_ready"), sem("merged_hi"), sem("merged_lo")
        x_ready = sem("x_updated")
        a_ready, c_ready, g_ready, f_ready, fh_ready, fl_ready = (sem(n) for n in ("a_padded", "conv_ready", "gelu_ready", "ff_ready", "ff_hi", "ff_lo"))
        act_c, dve_c = sem("scalar_chain"), sem("vector_chain")
        prol = sem("prologue_done")
        mat_s, mem0_s = sem("matrices_loaded"), [sem(f"first_memory_loaded{i}") for i in range(2)]
        qz_ready, qz_zero = sem("padded_queries_ready"), sem("queries_padded_with_zeros")
        carrier = sem("wait_carrier")

        ACT_PER, DVE_PER = PER["act"], PER["dve"]
        act_n, dve_n = [0], [0]

        block = ctx.enter_context(nc.Block())

        @block.sync
        def _(sp):
            sp.dma_start(con[:, 0:K_MASK], consts[:, 0:K_MASK]).then_inc(mat_s, 16)
            for j in range(2):
                sp.dma_start(memraw[:, 4 * j:4 * j + 4, :], mem_in[:, 4 * j:4 * j + 4, :]).then_inc(mem0_s[j], 16)
            for s in range(2):
                sp.dma_start(raw[:, s, :], w[s]).then_inc(loaded[s], 16)
            for j in range(2):
                sp.dma_start(x[:, 4 * j:4 * j + 4, :], x_in[:, 4 * j:4 * j + 4, :]).then_inc(x_in_s, 16)
            for s in range(2, 4):
                sp.dma_start(raw[:, s, :], w[s]).then_inc(loaded[s], 16)
            sp.dma_start(con[:, K_MASK:NCON], consts[:, K_MASK:NCON]).then_inc(con_s, 16)
            sp.dma_start(fg[:, :], final_g).then_inc(fg_s, 16)
            with sp.Fori(1, DEPTH * UNITS // 4) as i:
                for s in range(4):
                    src = w[sp.snap(i * 4 + s)]
                    sp.wait_ge(hi_ready, i * 4 + s - 3)
                    sp.wait_ge(lo_ready, i * 4 + s - 3)
                    sp.dma_start(raw[:, s, :], src).then_inc(loaded[s], 16)

        @block.gpsimd
        def _(pool):
            def lo(u, s, l, iv=0):
                pool.wait_ge(hi_ready, l * UNITS + iv + u + 1)
                pool.wait_ge(unit_done, l * UNITS + iv + u - 1)
                pool.tensor_tensor(out=wlo[:, s % 2, :], in0=raw[:, s, :], in1=whi[:, s, :].bitcast(f32),
                                   op=ALU.subtract).then_inc(lo_ready, 1)

            with pool.Fori(0, DEPTH) as l:
                pool.wait_ge(hi_ready, l * UNITS + 1)
                pool.sem_inc(lo_ready, 1)
                pool.wait_ge(hi_ready, l * UNITS + 2)
                pool.tensor_tensor(out=wlo[:, 1, :], in0=raw[:, 1, :], in1=whi[:, 1, :].bitcast(f32),
                                   op=ALU.subtract).then_inc(lo_ready, 1)
                lo(2, 2, l)
                lo(3, 3, l)
                with pool.Fori(1, UNITS // 4) as i:
                    for s in range(4):
                        lo(s, s, l, i * 4)

        @block.scalar
        def _(act):
            l = [0]

            def link(ins):
                act_n[0] += 1
                ins.then_inc(act_c, 1)
                return ins

            def wait_chain():
                act.wait_ge(act_c, l[0] * ACT_PER + act_n[0])

            def hi(u, iv=0):
                s = u % 4
                act.wait_ge(loaded[s], (l[0] * UNITS + iv + (u - s)) * 4 + 16)
                if not (isinstance(iv, int) and iv + u < 4):
                    act.wait_ge(unit_done, l[0] * UNITS + iv + u - 3)
                nc.scalar.activation(whi[:, s, :], raw[:, s, :], ACT.Copy).then_inc(hi_ready, 1)

            def done(u, iv=0):
                act.wait_ge(unit_done, l[0] * UNITS + iv + u + 1)

            def squares(j, base):
                act.wait_ge(sq_used, l[0] * 16 + base + j - 1)
                nc.scalar.activation(sq[:, j % 2, :], x[:, j, :], ACT.Square).then_inc(sq_ready, 1)

            def rms(bank, n):
                act.wait_ge(sq_used, n)
                nc.scalar.activation(rs[:, :], bank[:, 0:T], ACT.Sqrt, bias=zp[:, 0:1], scale=1.0 / D_MODEL).then_inc(rs_ready, 1)

            act.wait_ge(prol, 2)
            for j in range(KT_):
                act.wait_ge(mem0_s[j // 4], 16)
                if j >= 2:
                    act.wait_ge(sq_used, j - 1)
                nc.scalar.activation(sq[:, j % 2, 0:MEM], memraw[:, j, :], ACT.Square).then_inc(sq_ready, 1)
            act.wait_ge(sq_used, 8)
            nc.scalar.activation(rs[:, 0:MEM], B[0][:, 0:MEM], ACT.Sqrt, bias=zp[:, 0:1], scale=1.0 / D_MODEL).then_inc(rs_ready, 1)
            act.wait_ge(x_in_s, 32)
            for j in range(4):
                act.wait_ge(sq_used, 8 + j - 1)
                nc.scalar.activation(sq[:, j % 2, :], x[:, j, :], ACT.Square).then_inc(sq_ready, 1)
            act.wait_ge(rs_ready, 1)
            act.wait_ge(prol, 3)

            with act.Fori(0, DEPTH) as lv:
                l[0] = lv
                act.wait_ge(loaded[0], (lv * UNITS) * 4 + 16)
                nc.scalar.activation(par[:, :], raw[:, 0, 0:NPAR], ACT.Copy).then_inc(hi_ready, 1)
                for b in range(4):
                    act.dma_start(cache[:, b, :], cache_k[lv, b]).then_inc(cache_s[b], 16)
                hi(1)
                hi(2)
                for m in (4, 5):
                    act.wait_ge(x_ready, lv * 24 + 16 + m + 1)
                    squares(m, 8)
                for j in range(KT_):
                    act.wait_ge(mf_ready, lv * 8 + j + 1)
                    nc.scalar.activation(hh[:, j, 0:MEM], memraw[:, j, :], ACT.Copy).then_inc(mh_ready, 1)
                hi(3)
                for m in (6, 7):
                    act.wait_ge(x_ready, lv * 24 + 16 + m + 1)
                    squares(m, 8)
                hi(4)
                done(U_MK)
                nc.scalar.activation(memK[:, 0, :], A[U_MK % 2][:, 0:MEM], ACT.Copy).then_inc(evac, 1)
                hi(U_MK + 4)
                rms(C[1], lv * 16 + 16)
                done(U_MK + 1)
                nc.scalar.activation(memK[:, 1, :], A[(U_MK + 1) % 2][:, 0:MEM], ACT.Copy).then_inc(evac, 1)
                hi(U_MK + 5)
                for h in range(2, 4):
                    u = U_MK + h
                    done(u)
                    nc.scalar.activation(memK[:, h, :], A[u % 2][:, 0:MEM], ACT.Copy).then_inc(evac, 1)
                    hi(u + 4)
                act.wait_ge(evac, lv * EVACS + 4)
                act.dma_start(mk_out[lv], memK).then_inc(out_s["mk"], 16)
                for u in range(U_MV, U_GA):
                    done(u)
                    if u == U_GA - 1:
                        for mtile in range(2):
                            nc.scalar.activation(memV[:, mtile, :], B[mtile][:, :], ACT.Copy).then_inc(memv_ready, 1)
                    hi(u + 4)
                    for j in (2 * (u - U_MV), 2 * (u - U_MV) + 1):
                        act.wait_ge(hf_ready, lv * 16 + j + 1)
                        nc.scalar.activation(oh[:, j, :], hf[:, j, :], ACT.Copy).then_inc(hh_ready, 1)
                act.wait_ge(memv_ready, lv * 2 + 2)
                act.dma_start(mv_out[lv], memV).then_inc(out_s["mv"], 16)
                done(U_GA)
                nc.scalar.activation(tmpa[0:LOWRANK, 0, :], A[U_GA % 2][0:LOWRANK, 0:T], ACT.Copy).then_inc(evac, 1)
                hi(U_GA + 4)
                for h in range(4):
                    u = U_XQ + h
                    done(u)
                    nc.scalar.activation(xq[:, h, :], A[u % 2][:, 0:T], ACT.Copy).then_inc(evac, 1)
                    hi(u + 4)

                def xexp_(e):
                    act.wait_ge(xmax, lv * 5 + e + 1)
                    if e >= 2:
                        act.wait_ge(xpt, lv * 5 + e - 1)
                    bank = B[e] if e < 4 else C[1]
                    for a in range(2):
                        i = nc.scalar.activation(pp[:, e % 2, a, :], bank[:, a * MEM:(a + 1) * MEM], ACT.Exp,
                                                 bias=sml[:, 4 * e + 2 + a:4 * e + 3 + a], scale=XSCALE,
                                                 accum_out=sml[:, 20 + 2 * e + a:21 + 2 * e + a])
                    i.then_inc(xexp, 1)

                def xturn(e):
                    act.wait_ge(xpt, lv * 5 + e + 1)
                    if e >= 2:
                        act.wait_ge(xo_done, lv * 5 + e - 1)
                    bank = B[e] if e < 4 else C[1]
                    nc.scalar.activation(pT[:, e % 2].rearrange("p a b -> p (a b)"), bank[:, :], ACT.Copy).then_inc(xpt_ready, 1)

                def xhi(e):
                    act.wait_ge(xo_done, lv * 5 + e + 1)
                    if e < 4:
                        i = nc.scalar.activation(oh[:, 8 + e, 0:SEQ], B[e][:, 0:SEQ], ACT.Copy)
                    else:
                        i = nc.scalar.activation(oh[:, 8:12, SEQ:T], C[1][:, 0:256].rearrange("p (h t) -> p h t", h=4), ACT.Copy)
                    i.then_inc(xoh, 1)

                def load_k(b):
                    act.wait_ge(xk_used, lv * 8 + b - 3)
                    act.dma_start(cache[:, b % 4, :], cache_k[lv, b]).then_inc(cache_s[b % 4], 16)

                def load_v(b):
                    if b < 4:
                        act.wait_ge(xk_used, lv * 8 + b + 5)
                    else:
                        act.wait_ge(xv_used, lv * 7 + b - 3)
                    act.dma_start(cache[:, b % 4, :], cache_v[lv, b]).then_inc(cache_s[b % 4], 16)

                def qk(i, dst):
                    u = U_QK + i
                    done(u)
                    nc.scalar.activation(dst, A[u % 2][:, 0:T], ACT.Copy).then_inc(evac, 1)
                    hi(u + 4)

                xexp_(0)
                xexp_(1)
                qk(0, kd[:, 0, :])
                qk(1, kd[:, 1, :])
                for p in range(2):
                    act.wait_ge(z_done, lv * 2 + p + 1)
                    link(nc.scalar.activation(zsb[:, p, :], C[p][:, 0:T], ACT.Identity, bias=par[:, C_AB + p:C_AB + p + 1]))
                wait_chain()
                for p in range(2):
                    link(nc.scalar.activation(ln1[:, p, :], zsb[:, p, :], ACT.Abs))
                wait_chain()
                for p in range(2):
                    link(nc.scalar.activation(bcum[:, p, :], ln1[:, p, :], ACT.Exp, scale=-1.0))
                wait_chain()
                for p in range(2):
                    nc.scalar.activation(ln1[:, p, :], bcum[:, p, :], ACT.Ln, bias=1.0).then_inc(ln_ready, 1)
                qk(2, qd[:, 0, :])
                qk(3, qd[:, 1, :])
                xturn(0)
                xturn(1)
                for p in range(2):
                    act.wait_ge(b_ready, lv * 2 + p + 1)
                    nc.scalar.activation(eb[:, p, :], bcum[:, p, :], ACT.Exp, scale=1.0 / 16)
                    nc.scalar.activation(enb[:, p, :], bcum[:, p, :], ACT.Exp, scale=-1.0 / 16)
                    nc.scalar.activation(ee[:, p, :], ee[:, p, :], ACT.Exp, scale=1.0 / 16).then_inc(eb_ready, 1)
                xexp_(2)
                xexp_(3)
                qk(4, kd[:, 2, :])
                load_k(4)
                load_k(5)
                qk(5, kd[:, 3, :])
                xhi(0)
                xhi(1)
                xturn(2)
                xturn(3)
                load_k(6)
                load_k(7)
                qk(6, qd[:, 2, :])
                load_v(0)
                load_v(1)
                qk(7, qd[:, 3, :])
                xhi(2)
                xhi(3)
                load_v(2)
                load_v(3)
                act.wait_ge(xk_used, lv * 8 + 8)
                nc.scalar.activation(sS, C[1][:, :], ACT.Copy).then_inc(xst, 1)
                for u in (U_GV, U_GV + 1):
                    done(u)
                    hi(u + 4)
                xexp_(4)
                for u in (U_GV + 2, U_GV + 3):
                    done(u)
                    if u == U_RV - 1:
                        for a in range(3):
                            nc.scalar.activation(vt[:, 0, a, :], B[a][:, :], ACT.Copy).then_inc(v_ready, 1)
                    hi(u + 4)
                    if u == U_GV + 2:
                        xturn(4)
                for u in range(U_RV, U_SIL):
                    done(u)
                    if u == U_SIL - 1:
                        for a in range(3):
                            nc.scalar.activation(vt[:, 1, a, :], RB[a][:, :], ACT.Copy).then_inc(v_ready, 1)
                    hi(u + 4)
                    for p in ((0, 1, 2), (3,), (), ())[u - U_RV]:
                        act.wait_ge(kt_done, lv * 4 + p + 1)
                        nc.scalar.activation(kT[:, p].rearrange("p a b -> p (a b)"), B[p % 3][:, 0:3 * P], ACT.Copy).then_inc(kt_ready, 1)
                    if u < U_RV + 2:
                        load_v(4 + 2 * (u - U_RV))
                        load_v(5 + 2 * (u - U_RV))
                xhi(4)
                act.wait_ge(out_s["mk"], lv * 16 + 16)
                act.wait_ge(out_s["mv"], lv * 16 + 16)
                act.wait_ge(xol, lv * 5 + 5)
                for p in range(2):
                    act.dma_start(s0[:, p], st_in[lv, p]).then_inc(st_s[p], 16)

                def gated(u):
                    done(u)
                    if u < U_GATE:
                        i = u - U_SIL
                        nc.scalar.activation(sil[:, i, :], A[u % 2][:, 0:T], ACT.Sigmoid).then_inc(sig_ready, 1)
                    else:
                        j = u - U_GATE
                        nc.scalar.activation(G[:, j, :], A[u % 2][:, 0:T], ACT.Sigmoid,
                                             bias=par[:, C_BG + j:C_BG + j + 1]).then_inc(evac, 1)
                    hi(u + 4)

                for p in range(4):
                    u = U_SIL + 8 * p
                    gated(u)
                    gated(u + 1)
                    act.wait_ge(s_ready, lv * 4 + p + 1)
                    act.dma_start(pst_out[lv, p], S[:, NCH - 1, :]).then_inc(out_s["pst"], 16)
                    gated(u + 2)
                    if p >= 2:
                        act.wait_ge(o_done, lv * 4 + p + 1)
                        for j in range(2):
                            nc.scalar.activation(osb[:, PART[j]], C[j][:, 0:2 * (SEQ, NS)[j]], ACT.Copy).then_inc(osb_ready, 1)
                    gated(u + 3)
                    if p < 2:
                        act.wait_ge(o_done, lv * 4 + p + 1)
                    else:
                        act.wait_ge(xc_done, lv * 2 + p - 1)
                    for j in range(2):
                        nc.scalar.activation(gsq[:, PART[j]], C[j][:, 0:2 * (SEQ, NS)[j]], ACT.Square).then_inc(gsq_ready, 1)
                    gated(u + 4)
                    act.wait_ge(snew, lv * 4 + p + 1)
                    act.dma_start(sst_out[lv, p], s0[:, p % 2]).then_inc(out_s[f"sst{p % 2}"], 16)
                    act.wait_ge(gss_done, lv * 4 + p + 1)
                    for j in range(2):
                        nc.scalar.activation(gri[:, PART[j]], B[2 + j][:, 0:2 * (SEQ, NS)[j]], ACT.Sqrt, scale=1.0 / DV,
                                             bias=zp[:, 0:1] if p < 2 else zp[:, 1:2]).then_inc(gsr_ready, 1)
                    gated(u + 5)
                    gated(u + 6)
                    for j in range(2):
                        act.wait_ge(of_ready, lv * 8 + 2 * p + j + 1)
                        nc.scalar.activation(hh[:, 2 * p:2 * p + 2, TOK[j]], heads(of_[:, PART[j]]), ACT.Copy).then_inc(ohr, 1)
                    gated(u + 7)
                    act.wait_ge(out_s["pst"], lv * 64 + p * 16 + 16)
                    if p < 2:
                        act.wait_ge(out_s[f"sst{p}"], lv * 32 + 16)
                        act.dma_start(s0[:, p], st_in[lv, p + 2]).then_inc(st_s[p], 16)
                for mp in range(4):
                    for b in range(3):
                        hi_u = U_BR + 3 * mp + b
                        done(hi_u)
                        hi(hi_u + 4)
                    for mm in range(2):
                        m = 2 * mp + mm
                        act.wait_ge(mg_ready, lv * 8 + m + 1)
                        nc.scalar.activation(oh[:, m, :], mf[:, m, :], ACT.Copy).then_inc(mgh, 1)
                for m in range(KT_):
                    u = U_OUT + m
                    done(u)
                    hi(u + 4)
                    act.wait_ge(x_ready, lv * 24 + 24 + m + 1)
                    squares(m, 16)
                rms(B[3], lv * 16 + 24)
                for j in range(KT_):
                    act.wait_ge(hf_ready, lv * 16 + 8 + j + 1)
                    nc.scalar.activation(hh[:, j, :], hf[:, j, :], ACT.Copy).then_inc(hh_ready, 1)

                def up_pair(j, s, k, banks, u, iv):
                    a = banks[0]
                    done(u, iv)
                    av = apad[s]
                    sv = av[:, 258:338].rearrange("p (b t) -> p b t", b=8)
                    ps = a[:, SEQ:T].rearrange("p (b t) -> p b t", b=8)
                    act.wait_ge(f_ready, lv * FT + j - 1 + 8)
                    nc.scalar.activation(av[:, 2:258], a[:, 0:SEQ], ACT.Copy)
                    nc.scalar.activation(sv[:, :, 2:10], ps, ACT.Copy)
                    nc.scalar.activation(sv[:, :, 0:2], par[:, bass.ds(k * 16 + C_CS, 16)].rearrange("p (b t) -> p b t", b=8), ACT.Copy)
                    nc.scalar.activation(cout[:, k, 0:2], a[:, 254:256], ACT.Copy)
                    nc.scalar.activation(cout[:, k, 2:18].rearrange("p (b t) -> p b t", b=8), ps[:, :, 6:8], ACT.Copy).then_inc(a_ready, 1)

                def ups(u0, n, j0, banks):
                    with act.Fori(0, n // 2) as i:
                        for s in range(2):
                            u = u0 + 2 * s
                            up_pair(j0 + s + i * 2, s, i * 2 + (s + j0), banks[2 * s:2 * s + 2], u, i * 4)
                            hi(u + 4, i * 4)
                            act.wait_ge(c_ready, lv * FT + i * 2 + (j0 + s + 1))
                            nc.scalar.activation(gg[s][:, 0:336], cc[s][2][:, 0:336], ACT.Gelu_apprx_tanh).then_inc(g_ready, 1)
                            done(u + 1, i * 4)
                            hi(u + 5, i * 4)
                            act.wait_ge(f_ready, lv * FT + i * 2 + (j0 + s + 1) + 8)
                            nc.scalar.activation(oh[:, i * 2 + s, :], ff[:, s, :], ACT.Copy).then_inc(fh_ready, 1)

                ups(U_UP1, FA, 0, [A[0], A[1], C[0], C[1]])
                for u in range(U_DN1, U_UP2):
                    done(u)
                    hi(u + 4)
                ups(U_UP2, FB, FA, B)
                act.wait_ge(fh_ready, lv * FT + FT)
                act.dma_start(conv_out[lv], cout[:, :, :]).then_inc(out_s["conv"], 16)
                act.dma_start(memraw, mem_in).then_inc(mem_s, 16)
                for u in range(U_DN2, UNITS):
                    done(u)
                    if u + 4 < UNITS:
                        hi(u + 4)
                    if U_DN2 + 5 <= u < UNITS - 1:
                        m = u - U_DN2 - 5
                        act.wait_ge(x_ready, lv * 24 + 24 + 16 + m + 1)
                        squares(m, 24)
                act.wait_ge(out_s["conv"], lv * 16 + 16)
                act.wait_ge(mem_s, lv * 16 + 16)
                act.wait_ge(out_s["sst0"], lv * 32 + 32)
                act.wait_ge(out_s["sst1"], lv * 32 + 32)
                assert act_n[0] == ACT_PER
            l[0] = DEPTH
            for m in range(4, KT_):
                act.wait_ge(x_ready, DEPTH * 24 + 16 + m + 1)
                squares(m, 8)
            rms(C[1], DEPTH * 16 + 16)
            act.wait_ge(hf_ready, DEPTH * 16 + 8)
            act.dma_start(y_out, hf).then_inc(out_s["y"], 16)
            act.wait_ge(out_s["y"], 16)

        @block.vector
        def _(dve):
            l = [0]
            V = nc.vector

            def link(ins):
                dve_n[0] += 1
                ins.then_inc(dve_c, 1)
                dve.wait_ge(dve_c, l[0] * DVE_PER + dve_n[0])

            V.memset(zp[:, 0:1], EPS).then_inc(prol, 1)
            V.memset(zp[:, 1:2], GEPS).then_inc(prol, 1)
            dve.wait_ge(rs_ready, 1)
            V.reciprocal(rmem[:, :], rs[:, 0:MEM]).then_inc(prol, 1)
            dve.wait_ge(prol, 3)
            dve.wait_ge(mat_s, 16)
            dve.wait_ge(con_s, 16)
            dve.wait_ge(fg_s, 16)
            dve.wait_ge(x_in_s, 32)
            dve.sem_inc(x_ready, 24)
            for e in range(2):
                V.memset(qz[64 - 64 * e:128 - 64 * e, e, :], 0.0).then_inc(qz_zero, 1)
            dve.sem_inc(f_ready, 8)

            def norm(gain, rv, hv, xh, xl):
                dve.wait_ge(rs_ready, rv)
                link(V.reciprocal(rs[:, :], rs[:, :]))
                for j in range(KT_ + 1):
                    if j < KT_:
                        V.scalar_tensor_tensor(out=hf[:, j, :], in0=x[:, j, :], scalar=gain[:, j:j + 1], in1=rs[:, :],
                                               op0=ALU.mult, op1=ALU.mult).then_inc(hf_ready, 1)
                    if j and xh is not None:
                        dve.wait_ge(hh_ready, hv + j)
                        V.tensor_tensor(out=xl[:, j - 1, :], in0=hf[:, j - 1, :], in1=xh[:, j - 1, :].bitcast(f32),
                                        op=ALU.subtract).then_inc(hl_ready, 1)

            with dve.Fori(0, DEPTH) as lv:
                l[0] = lv
                dve.wait_ge(hi_ready, lv * UNITS + 1)
                for j in range(KT_ + 1):
                    if j < KT_:
                        V.scalar_tensor_tensor(out=memraw[:, j, :], in0=memraw[:, j, :], scalar=par[:, C_MN + j:C_MN + j + 1],
                                               in1=rmem[:, :], op0=ALU.mult, op1=ALU.mult).then_inc(mf_ready, 1)
                    if j:
                        dve.wait_ge(mh_ready, lv * 8 + j)
                        V.tensor_tensor(out=hl[:, j - 1, 0:MEM], in0=memraw[:, j - 1, :], in1=hh[:, j - 1, 0:MEM].bitcast(f32),
                                        op=ALU.subtract).then_inc(ml_ready, 1)
                norm(par[:, C_N1:C_N1 + 8], lv * 2 + 2, lv * 16, oh, ol)

                def xmaxes(e):
                    dve.wait_ge(xscore, lv * 5 + e + 1)
                    bank = B[e] if e < 4 else C[1]
                    link(V.tensor_reduce(out=sml[:, 4 * e:4 * e + 2], in_=bank[:, :].rearrange("p (a m) -> p a m", a=2),
                                         axis=AX.X, op=ALU.max))
                    V.tensor_scalar(sml[:, 4 * e + 2:4 * e + 4], sml[:, 4 * e:4 * e + 2], -XSCALE, None, ALU.mult).then_inc(xmax, 1)

                def xnorm(e):
                    dve.wait_ge(xexp, lv * 5 + e + 1)
                    link(V.reciprocal(sml[:, 30 + 2 * e:32 + 2 * e], sml[:, 20 + 2 * e:22 + 2 * e]))
                    for a in range(2):
                        i = V.tensor_scalar(pp[:, e % 2, a, :], pp[:, e % 2, a, :], sml[:, 30 + 2 * e + a:31 + 2 * e + a], None, ALU.mult)
                        if a == 0:
                            link(i)
                        else:
                            i.then_inc(xp_ready, 1)

                def xlo(e):
                    dve.wait_ge(xoh, lv * 5 + e + 1)
                    if e < 4:
                        o, i0, i1 = ol[:, 8 + e, 0:SEQ], B[e][:, 0:SEQ], oh[:, 8 + e, 0:SEQ]
                    else:
                        o, i0, i1 = ol[:, 8:12, SEQ:T], C[1][:, 0:256].rearrange("p (h t) -> p h t", h=4), oh[:, 8:12, SEQ:T]
                    V.tensor_tensor(out=o, in0=i0, in1=i1.bitcast(f32), op=ALU.subtract).then_inc(xol, 1)

                for e in range(4):
                    xmaxes(e)
                xnorm(0)
                xnorm(1)
                for p in range(2):
                    dve.wait_ge(ln_ready, lv * 2 + p + 1)
                    link(V.scalar_tensor_tensor(out=zsb[:, p, :], in0=zsb[:, p, :], scalar=0.0, in1=ln1[:, p, :],
                                                op0=ALU.min, op1=ALU.subtract))
                    link(V.tensor_tensor_scan(out=bcum[:, p, :], data0=con[:, K_RST:K_RST + T], data1=zsb[:, p, :],
                                              initial=0.0, op0=ALU.mult, op1=ALU.add))
                    for lo_, hi_, n in ((0, SEQ, CHUNK), (SEQ, T, DEC_SEQ)):
                        bv = bcum[:, p, lo_:hi_].rearrange("p (c t) -> p c t", t=n)
                        i = V.tensor_tensor(out=ee[:, p, lo_:hi_].rearrange("p (c t) -> p c t", t=n),
                                            in0=bv[:, :, n - 1:n].to_broadcast([P, (hi_ - lo_) // n, n]), in1=bv, op=ALU.subtract)
                        if n == CHUNK:
                            link(i)
                        else:
                            i.then_inc(b_ready, 1)
                for p in range(2):
                    dve.wait_ge(eb_ready, lv * 2 + p + 1)
                    dve.wait_ge(evac, lv * EVACS + 13)
                    V.tensor_tensor(out=ke[:, p, :], in0=kd[:, p, :], in1=ee[:, p, :], op=ALU.mult).then_inc(ke_ready, 1)
                    dve.wait_ge(ke_ready, lv * 4 + p + 1)
                    link(V.tensor_tensor(out=kd[:, p, :], in0=kd[:, p, :], in1=enb[:, p, :], op=ALU.mult))
                    link(V.tensor_copy(sml[:, 40 + 8 * p:48 + 8 * p], eb[:, p, 0:SEQ].rearrange("p (c t) -> p c t", t=CHUNK)[:, :, CHUNK - 1]))
                    link(V.tensor_copy(zdec[:, p, :], eb[:, p, SEQ:T].rearrange("p (c t) -> p c t", t=DEC_SEQ)[:, :, DEC_SEQ - 1]))
                    V.scalar_tensor_tensor(out=qd[:, p, :], in0=qd[:, p, :], scalar=float(DK) ** -0.5, in1=eb[:, p, :],
                                           op0=ALU.mult, op1=ALU.mult).then_inc(qd_ready, 1)
                xnorm(2)
                xnorm(3)
                xlo(0)
                xlo(1)

                def rope(r):
                    p, buf = 2 + r % 2, kd if r < 2 else qd
                    if r == 3:
                        dve.wait_ge(qd_ready, lv * 4 + 3)
                    elif r:
                        dve.wait_ge(ke_ready, lv * 4 + r + 2)
                    dve.wait_ge(rot_done, lv * 4 + r + 1)
                    V.tensor_tensor(out=rt[:, 0, :], in0=C[0][:, 0:T], in1=con[:, K_SIN:K_SIN + T], op=ALU.mult).then_inc(rot_used, 1)
                    link(V.tensor_tensor(out=rt[:, 1, :], in0=buf[:, p, :], in1=con[:, K_COS:K_COS + T], op=ALU.mult))
                    link(V.tensor_tensor(out=rt[:, 0, :], in0=rt[:, 0, :], in1=rt[:, 1, :], op=ALU.add))
                    dd = (K_DK if r < 2 else K_DQ) + (p - 2) * T
                    i = V.tensor_tensor(out=buf[:, p, :], in0=rt[:, 0, :], in1=con[:, dd:dd + T], op=ALU.mult)
                    if r >= 2:
                        i.then_inc(qd_ready, 1)
                        return
                    link(i)
                    link(V.tensor_scalar(ke[:, p, 0:SEQ], kd[:, p, 0:SEQ], con[:, K_DE + 2 * (p - 2):K_DE + 2 * (p - 2) + 1], None, ALU.mult))
                    V.tensor_scalar(ke[:, p, SEQ:T], kd[:, p, SEQ:T], con[:, K_DE + 2 * (p - 2) + 1:K_DE + 2 * (p - 2) + 2], None,
                                    ALU.mult).then_inc(ke_ready, 1)

                rope(0)
                xlo(2)
                xlo(3)
                rope(1)
                xmaxes(4)
                xnorm(4)
                rope(2)
                rope(3)

                def silu(i):
                    dve.wait_ge(sig_ready, lv * 8 + i + 1)
                    V.scalar_tensor_tensor(out=sil[:, i, :], in0=sil[:, i, :], scalar=par[:, C_ON + i:C_ON + i + 1],
                                           in1=A[(U_SIL + i) % 2][:, 0:T], op0=ALU.mult, op1=ALU.mult).then_inc(sil_ready, 1)

                def pair_operands(p):
                    dve.wait_ge(qd_ready, lv * 4 + p + 1)
                    for e in range(2):
                        V.tensor_copy(qz[64 * e:64 * e + 64, e, :], qd[64 * e:64 * e + 64, p, :]).then_inc(qz_ready, 1)
                    dve.wait_ge(kt_ready, lv * 4 + p + 1)
                    for a in range(2):
                        V.tensor_tensor(out=kTc[:, 4 * a:4 * a + 4, :], in0=kT[:, p, a:a + 1, :].to_broadcast([P, 4, P]),
                                        in1=con[:, K_CM:K_CM + 4].rearrange("p (b o) -> p b o", o=1).to_broadcast([P, 4, P]),
                                        op=ALU.mult).then_inc(ktc_ready, 1)
                    V.tensor_tensor(out=kTm[64:128, :, :], in0=kT[64:128, p, 2:3, :].to_broadcast([64, 8, P]),
                                    in1=con[64:128, K_BM:K_BM + 8].rearrange("p (b o) -> p b o", o=1).to_broadcast([64, 8, P]),
                                    op=ALU.mult).then_inc(ktm_ready, 1)

                link(V.memset(scm[:, :], 0.0))
                mask = con[:, K_MASK:K_MASK + T].bitcast(u32)
                pair_operands(0)
                xlo(4)
                for p in range(4):
                    if p == 0:
                        silu(0)
                    dve.wait_ge(up_done, lv * 4 + p + 1)
                    if p:
                        dve.wait_ge(out_s["pst"], lv * 64 + p * 16)
                    for c in range(NCH):
                        upd = B[c // 4][:, (c % 4) * P:(c % 4) * P + P]
                        if p < 2:
                            dec = sml[:, 40 + 8 * p + c:41 + 8 * p + c]
                        else:
                            dec = con[:, K_DE + 2 * (p - 2):K_DE + 2 * (p - 2) + 1]
                        if c == 0:
                            i = V.tensor_copy(S[:, 0, :], upd)
                        else:
                            i = V.scalar_tensor_tensor(out=S[:, c, :], in0=S[:, c - 1, :], scalar=dec, in1=upd, op0=ALU.mult, op1=ALU.add)
                        if c < NCH - 1:
                            link(i)
                        else:
                            i.then_inc(s_ready, 1)
                    dve.wait_ge(sc_done, lv * 4 + p + 1)
                    dve.sem_inc(carrier, 1)
                    for e in range(2):
                        V.copy_predicated(scm[:, e * SEQ:(e + 1) * SEQ], mask[:, 0:SEQ], C[0][:, e * SEQ:(e + 1) * SEQ]).then_inc(scm_ready, 1)
                        V.copy_predicated(scm[:, 2 * SEQ + e * NS:2 * SEQ + (e + 1) * NS], mask[:, SEQ:T],
                                          C[1][:, e * NS:(e + 1) * NS]).then_inc(scm_ready, 1)
                    if p == 0:
                        for i in range(1, 4):
                            silu(i)
                    dve.wait_ge(us_done, lv * 4 + p + 1)
                    for b in range(DEC_BATCH):
                        upd = B[2 + b // 4][:, (b % 4) * P:(b % 4) * P + P]
                        dec = zdec[:, p, b:b + 1] if p < 2 else con[:, K_DE + 2 * (p - 2) + 1:K_DE + 2 * (p - 2) + 2]
                        i = V.scalar_tensor_tensor(out=s0[:, p % 2, b, :], in0=s0[:, p % 2, b, :], scalar=dec, in1=upd, op0=ALU.mult, op1=ALU.add)
                        if b < 7:
                            link(i)
                        else:
                            i.then_inc(snew, 1)
                    if p == 0:
                        silu(4)
                        silu(5)
                    if p < 3:
                        pair_operands(p + 1)
                    if p:
                        dve.wait_ge(olr, lv * 8 + 2 * p)
                    for j in range(2):
                        dve.wait_ge(gsr_ready, lv * 8 + 2 * p + j + 1)
                        link(V.reciprocal(gri[:, PART[j]], gri[:, PART[j]]))
                        if p == 0 and j == 0:
                            silu(6)
                        link(V.tensor_tensor(out=of_[:, PART[j]], in0=C[j][:, 0:2 * (SEQ, NS)[j]], in1=gri[:, PART[j]], op=ALU.mult))
                        V.tensor_tensor(out=heads(of_[:, PART[j]]), in0=heads(of_[:, PART[j]]), in1=sil[:, 2 * p:2 * p + 2, TOK[j]],
                                        op=ALU.mult).then_inc(of_ready, 1)
                    if p == 0:
                        silu(7)
                    for j in range(2):
                        dve.wait_ge(ohr, lv * 8 + 2 * p + j + 1)
                        V.tensor_tensor(out=hl[:, 2 * p:2 * p + 2, TOK[j]], in0=heads(of_[:, PART[j]]), in1=hh[:, 2 * p:2 * p + 2, TOK[j]].bitcast(f32),
                                        op=ALU.subtract).then_inc(olr, 1)
                dve.wait_ge(evac, lv * EVACS + 41)
                BR = [A, C, B]
                for mp in range(4):
                    for b in range(3):
                        dve.wait_ge(unit_done, lv * UNITS + U_BR + 3 * mp + b + 1)
                        for mm in range(2):
                            m = 2 * mp + mm
                            V.tensor_tensor(out=(acc if b == 0 else mt)[:, mm, :], in0=BR[b][mm][:, 0:T], in1=G[:, 8 * b + m, :],
                                            op=ALU.mult).then_inc(br_used, 1)
                        dve.wait_ge(br_used, lv * 24 + 6 * mp + 2 * b + 2)
                        if b == 1:
                            for mm in range(2):
                                link(V.tensor_tensor(out=acc[:, mm, :], in0=acc[:, mm, :], in1=mt[:, mm, :], op=ALU.add))
                        if b == 2:
                            for mm in range(2):
                                m = 2 * mp + mm
                                V.tensor_tensor(out=mf[:, m, :], in0=acc[:, mm, :], in1=mt[:, mm, :], op=ALU.add).then_inc(mg_ready, 1)
                            for mm in range(2):
                                m = 2 * mp + mm
                                dve.wait_ge(mgh, lv * 8 + m + 1)
                                V.tensor_tensor(out=ol[:, m, :], in0=mf[:, m, :], in1=oh[:, m, :].bitcast(f32),
                                                op=ALU.subtract).then_inc(mgl, 1)
                for m in range(KT_):
                    dve.wait_ge(unit_done, lv * UNITS + U_OUT + m + 1)
                    V.tensor_tensor(out=x[:, m, :], in0=x[:, m, :], in1=A[m % 2][:, 0:T], op=ALU.add).then_inc(x_ready, 1)
                norm(par[:, C_N2:C_N2 + 8], lv * 2 + 3, lv * 16 + 8, hh, hl)
                for s in range(2):
                    link(V.memset(apad[s][:, 0:2], 0.0))

                def ups(j0, n, banks, u0):
                    base = dve_n[0]
                    dve.sem_inc(carrier, 1)
                    with dve.Fori(0, n // 2) as i:
                        def lk(ins, k):
                            ins.then_inc(dve_c, 1)
                            dve.wait_ge(dve_c, lv * DVE_PER + i * 6 + (base + k))
                        for s in range(2):
                            jw = i * 2 + (j0 + s)
                            dve.wait_ge(a_ready, lv * FT + i * 2 + (j0 + s + 1))
                            cw = lambda t: par[:, bass.ds(jw + (C_CW + t * FT), 1)]
                            lk(V.tensor_scalar(cc[s][0][:, 0:336], apad[s][:, 0:336], cw(0), par[:, bass.ds(jw + C_CB, 1)], ALU.mult, ALU.add), 3 * s + 1)
                            lk(V.scalar_tensor_tensor(out=cc[s][1][:, 0:336], in0=apad[s][:, 1:337], scalar=cw(1), in1=cc[s][0][:, 0:336],
                                                      op0=ALU.mult, op1=ALU.add), 3 * s + 2)
                            V.scalar_tensor_tensor(out=cc[s][2][:, 0:336], in0=apad[s][:, 2:338], scalar=cw(2), in1=cc[s][1][:, 0:336],
                                                   op0=ALU.mult, op1=ALU.add).then_inc(c_ready, 1)
                            dve.wait_ge(g_ready, lv * FT + i * 2 + (j0 + s + 1))
                            dve.wait_ge(unit_done, lv * UNITS + i * 4 + (u0 + 2 * s + 2))
                            bb = banks[2 * s + 1]
                            lk(V.tensor_tensor(out=ff[:, s, 0:SEQ], in0=gg[s][:, 0:SEQ], in1=bb[:, 0:SEQ], op=ALU.mult), 3 * s + 3)
                            V.tensor_tensor(out=ff[:, s, SEQ:T].rearrange("p (b t) -> p b t", b=8),
                                            in0=gg[s][:, 258:338].rearrange("p (b t) -> p b t", b=8)[:, :, 0:8],
                                            in1=bb[:, SEQ:T].rearrange("p (b t) -> p b t", b=8), op=ALU.mult).then_inc(f_ready, 1)
                            dve.wait_ge(fh_ready, lv * FT + i * 2 + (j0 + s + 1))
                            V.tensor_tensor(out=ol[:, i * 2 + s, :], in0=ff[:, s, :], in1=oh[:, i * 2 + s, :].bitcast(f32),
                                            op=ALU.subtract).then_inc(fl_ready, 1)
                            dve.wait_ge(fl_ready, lv * FT + i * 2 + (j0 + s + 1))
                    dve_n[0] = base + 6 * (n // 2)

                def downs(u_q0, u_q1, banks):
                    for q, u in ((0, u_q0), (1, u_q1)):
                        dve.wait_ge(unit_done, lv * UNITS + u)
                        for mm in range(4):
                            V.tensor_tensor(out=x[:, 4 * q + mm, :], in0=x[:, 4 * q + mm, :], in1=banks[q][mm][:, 0:T],
                                            op=ALU.add).then_inc(x_ready, 1)

                AC = [A[0], A[1], C[0], C[1]]
                ups(0, FA, AC, U_UP1)
                downs(U_DN1 + 6, U_UP2, [B, AC])
                ups(FA, FB, B, U_UP2)
                downs(U_DN2 + 5, UNITS, [AC, B])
                assert dve_n[0] == DVE_PER
            l[0] = DEPTH
            dve_n[0] = 0
            norm(fg, DEPTH * 2 + 2, 0, None, None)

        @block.tensor
        def _(pe):
            l = [0]
            MM = nc.tensor.matmul

            def ready(u, iv=0):
                pe.wait_ge(hi_ready, l[0] * UNITS + iv + u + 1)
                pe.wait_ge(lo_ready, l[0] * UNITS + iv + u + 1)

            def three(out, s, c, n, xh, xl, first, last, flip=False):
                wh, wl = whi[:, s % 4, c:c + n], wlo[:, s % 2, c:c + n]
                prods = ((wh, xh), (wh, xl), (wl, xh))
                for i, (a, b) in enumerate(prods):
                    if flip:
                        a, b = b, a
                    r = MM(out, a, b, start=first and i == 0, stop=last and i == 2, skip_group_check=True)
                return r

            def wait_bank(u):
                if U_MK + 2 <= u < U_MV:
                    pe.wait_ge(evac, l[0] * EVACS + u - 2)
                elif u == U_GA:
                    pe.wait_ge(evac, l[0] * EVACS + 4)
                elif U_XQ <= u < U_GV:
                    pe.wait_ge(evac, l[0] * EVACS + (u - U_GA) + 3)
                elif U_SIL <= u < U_SIL + 2:
                    pe.wait_ge(evac, l[0] * EVACS + 17)
                elif U_SIL + 2 <= u < U_GATE + 2:
                    pe.wait_ge(sil_ready, l[0] * 8 + u - U_SIL - 1)
                elif U_GATE + 2 <= u < U_BR:
                    pe.wait_ge(evac, l[0] * EVACS + 17 + u - U_GATE - 1)
                elif U_OUT <= u < U_OUT + 2:
                    pe.wait_ge(br_used, l[0] * 24 + 24)
                elif U_OUT + 2 <= u < U_UP1:
                    pe.wait_ge(x_ready, l[0] * 24 + 24 + u - U_OUT - 1)

            def unit(u, xh, xl, n, first_wait=None, small=None):
                wait_bank(u)
                ready(u)
                for k in range(KT_):
                    if first_wait is not None:
                        pe.wait_ge(first_wait[0], first_wait[1] + k + 1)
                    wh, wl, o = whi[:, u % 4, k * P:(k + 1) * P], wlo[:, u % 2, k * P:(k + 1) * P], A[u % 2][:, 0:n]
                    for i, (a, b) in enumerate(((wh, xh), (wh, xl), (wl, xh))):
                        r = MM(o, a, b[:, k, 0:n], start=k == 0 and i == 0, stop=k == KT_ - 1 and i == 2, skip_group_check=True)
                        if small is not None and k * 3 + i < 23:
                            small(k * 3 + i)
                r.then_inc(unit_done, 1)

            def vunit(u, i, xh, xl, toks, banks, small=None):
                ready(u)
                for kk in range(2):
                    k = 2 * i + kk
                    wh, wl = whi[:, u % 4, kk * 512:(kk + 1) * 512], wlo[:, u % 2, kk * 512:(kk + 1) * 512]
                    for a, t0 in enumerate(toks):
                        for j, (x_, w_) in enumerate(((xh, wh), (xl, wh), (xh, wl))):
                            r = MM(banks[a][:, :], x_[:, k, t0:t0 + P], w_, start=k == 0 and j == 0, stop=k == KT_ - 1 and j == 2,
                                   skip_group_check=True)
                            n = kk * 3 * len(toks) + 3 * a + j
                            if small is not None and n < 17:
                                small(n)
                r.then_inc(unit_done, 1)

            def sumsq(j, n, bank, width=T):
                pe.wait_ge(sq_ready, n)
                MM(bank[:, 0:width], ones, sq[:, j % 2, 0:width], start=j == 0, stop=j == KT_ - 1).then_inc(sq_used, 1)

            pe.wait_ge(mat_s, 16)
            for j in range(KT_):
                sumsq(j, j + 1, B[0], MEM)
            for j in range(4):
                sumsq(j, 8 + j + 1, C[1])

            with pe.Fori(0, DEPTH) as lv:
                l[0] = lv
                pe.wait_ge(hi_ready, lv * UNITS + 1)
                pe.sem_inc(unit_done, 1)
                for h in range(4):
                    unit(U_MK + h, hh, hl, MEM, (ml_ready, lv * 8) if h == 0 else None)
                    if h < 2:
                        sumsq(4 + 2 * h, lv * 16 + 13 + 2 * h, C[1])
                        sumsq(5 + 2 * h, lv * 16 + 14 + 2 * h, C[1])
                for i in range(4):
                    vunit(U_MV + i, i, hh, hl, (0, P), B)
                unit(U_GA, oh, ol, T, (hl_ready, lv * 16))
                for h in range(4):
                    unit(U_XQ + h, oh, ol, T)

                pe.wait_ge(memv_ready, lv * 2 + 2)
                pe.wait_ge(evac, lv * EVACS + 9)
                for e in range(4):
                    for a in range(2):
                        r = MM(B[e][:, a * MEM:(a + 1) * MEM], xq[:, e, a * P:(a + 1) * P], memK[:, e, :], start=True, stop=True,
                               skip_group_check=True)
                    r.then_inc(xscore, 1)

                def turn(e):
                    pe.wait_ge(xp_ready, lv * 5 + e + 1)
                    bank = B[e] if e < 4 else C[1]
                    for m in range(2):
                        for a in range(2):
                            r = nc.tensor.transpose(bank[:, m * MEM + a * P:m * MEM + (a + 1) * P], pp[:, e % 2, a, m * P:(m + 1) * P], ident)
                    r.then_inc(xpt, 1)

                def pv(e):
                    pe.wait_ge(xpt_ready, lv * 5 + e + 1)
                    for m in range(2):
                        r = MM(B[e][:, 0:SEQ], memV[:, m, e * P:(e + 1) * P], pT[:, e % 2, m, :], start=m == 0, stop=m == 1, skip_group_check=True)
                    r.then_inc(xo_done, 1)

                def sample_scores(b0, i):
                    if i >= 16:
                        return
                    b, h, m = b0 + i // 8, i // 2 % 4, i % 2
                    if i % 8 == 0:
                        pe.wait_ge(cache_s[b % 4], lv * 64 + 16 * (1 + b // 4))
                    o = m * 256 + b * 32 + h * 8
                    r = MM(C[1][:, o:o + 8], cache[:, b % 4, h * MEM + m * P:h * MEM + (m + 1) * P], xq[:, h, SEQ + 8 * b:SEQ + 8 * b + 8],
                           start=True, stop=True, skip_group_check=True)
                    if i % 8 == 7:
                        r.then_inc(xk_used, 1)

                def sample_values(b0, i):
                    if i >= 16:
                        return
                    b, h, m = b0 + i // 8, i // 2 % 4, i % 2
                    if i % 8 == 0:
                        pe.wait_ge(cache_s[b % 4], lv * 64 + 16 * (3 + b // 4))
                    o = h * 64 + b * 8
                    r = MM(C[1][:, o:o + 8], cache[:, b % 4, m * 512 + h * P:m * 512 + (h + 1) * P],
                           pT[:, 0, m, b * 32 + h * 8:b * 32 + h * 8 + 8], start=m == 0, stop=m == 1, skip_group_check=True)
                    if i % 8 == 7:
                        r.then_inc(xo_done if b == 7 else xv_used, 1)

                def rot(r):
                    buf = (kd if r < 2 else qd)[:, 2 + r % 2, :]
                    pe.wait_ge(evac, lv * EVACS + 9 + 4 + r + 1)
                    if r:
                        pe.wait_ge(rot_used, lv * 4 + r)
                    else:
                        pe.wait_ge(b_ready, lv * 2 + 1)
                    MM(C[0][:, 0:T], perm, buf, start=True, stop=True).then_inc(rot_done, 1)

                unit(U_QK, oh, ol, T)
                unit(U_QK + 1, oh, ol, T)
                for p in range(2):
                    MM(C[p][:, 0:T], par[0:LOWRANK, C_AU + p * P:C_AU + (p + 1) * P], tmpa[0:LOWRANK, 0, :], start=True, stop=True).then_inc(z_done, 1)
                unit(U_QK + 2, oh, ol, T)
                unit(U_QK + 3, oh, ol, T)
                turn(0)
                turn(1)
                pe.wait_ge(ln_ready, lv * 2 + 2)
                unit(U_QK + 4, oh, ol, T, small=lambda i: sample_scores(0, i))
                unit(U_QK + 5, oh, ol, T, small=lambda i: sample_scores(2, i))
                pv(0)
                pv(1)
                turn(2)
                turn(3)
                unit(U_QK + 6, oh, ol, T, small=lambda i: sample_scores(4, i))
                rot(0)
                unit(U_QK + 7, oh, ol, T, small=lambda i: sample_scores(6, i))
                pv(2)
                pv(3)
                rot(1)
                toks = (0, P, T - P)
                pe.wait_ge(xol, lv * 5 + 3)
                vunit(U_GV, 0, oh, ol, toks, B)
                pe.wait_ge(xst, lv + 1)
                for a in range(2):
                    for m in range(2):
                        r = nc.tensor.transpose(C[1][:, a * MEM + m * P:a * MEM + (m + 1) * P], sS[:, m * 256 + a * P:m * 256 + (a + 1) * P], ident)
                r.then_inc(xscore, 1)
                vunit(U_GV + 1, 1, oh, ol, toks, B)
                vunit(U_GV + 2, 2, oh, ol, toks, B)
                rot(2)
                turn(4)
                vunit(U_GV + 3, 3, oh, ol, toks, B)
                rot(3)
                pe.wait_ge(xpt_ready, lv * 5 + 5)
                pe.wait_ge(evac, lv * EVACS + 17)
                pe.wait_ge(xol, lv * 5 + 4)

                def turn_keys(p):
                    pe.wait_ge(ke_ready, lv * 4 + p + 1)
                    for a, t0 in enumerate(toks):
                        r = nc.tensor.transpose(B[p % 3][:, a * P:(a + 1) * P], ke[:, p, t0:t0 + P], ident)
                    r.then_inc(kt_done, 1)

                for i in range(4):
                    vunit(U_RV + i, i, oh, ol, toks, RB, lambda n: sample_values(2 * i, n))
                    if i == 0:
                        pe.wait_ge(v_ready, lv * 6 + 3)
                        for p in range(3):
                            turn_keys(p)
                    if i == 1:
                        pe.wait_ge(kt_ready, lv * 4 + 1)
                        turn_keys(3)
                pe.wait_ge(v_ready, lv * 6 + 6)

                def gated(u, small=None):
                    unit(u, oh, ol, T, small=small)

                def chunk_update(p, i):
                    if i >= 2 * NCH:
                        return
                    c, e = i // 2, i % 2
                    h = 2 * (p % 2) + e
                    r = MM(B[c // 4][64 * e:64 * e + 64, (c % 4) * P:(c % 4) * P + P], kTc[:, c, 64 * e:64 * e + 64],
                           vt[:, p // 2, c // 4, h * P:(h + 1) * P], start=True, stop=True, skip_group_check=True)
                    if i == 2 * NCH - 1:
                        r.then_inc(up_done, 1)

                def sample_update(p, i):
                    if i >= 2 * DEC_BATCH:
                        return
                    b, e = i // 2, i % 2
                    h = 2 * (p % 2) + e
                    r = MM(B[2 + b // 4][64 * e:64 * e + 64, (b % 4) * P:(b % 4) * P + P], kTm[64:128, b, 64 * e:64 * e + 64],
                           vt[64:128, p // 2, 2, h * P:(h + 1) * P], start=True, stop=True, skip_group_check=True, tile_position=(64, 64 * e))
                    if i == 2 * DEC_BATCH - 1:
                        r.then_inc(us_done, 1)

                def output(p, i):
                    if i < 6:
                        e, a = i % 2, i // 2
                        h = 2 * (p % 2) + e
                        if a < 2:
                            o, t0 = C[0][:, e * SEQ + a * P:e * SEQ + (a + 1) * P], e * SEQ + a * P
                            MM(o, vt[:, p // 2, a, h * P:(h + 1) * P], scm[:, t0:t0 + P], start=i == 0, stop=False, skip_group_check=True)
                        else:
                            t0 = 2 * SEQ + e * NS
                            MM(C[1][:, e * NS:(e + 1) * NS], vt[:, p // 2, 2, h * P:(h + 1) * P], scm[:, t0:t0 + NS], start=e == 0, stop=False,
                               skip_group_check=True)
                    elif i < 6 + NCH - 1:
                        c = i - 5
                        MM(heads(C[0][:, :])[:, :, c * CHUNK:(c + 1) * CHUNK], S[:, c - 1, :], qz[:, :, c * CHUNK:(c + 1) * CHUNK],
                           start=False, stop=c == NCH - 1, skip_group_check=True)
                    elif i < 6 + NCH - 1 + DEC_BATCH:
                        b = i - 6 - NCH + 1
                        r = MM(heads(C[1][:, 0:2 * NS])[:, :, 8 * b:8 * b + 8], s0[:, p % 2, b, :], qz[:, :, SEQ + 8 * b:SEQ + 8 * b + 8],
                               start=False, stop=b == 7, skip_group_check=True)
                        if b == 7:
                            r.then_inc(o_done, 1)

                pe.wait_ge(qz_zero, 2)
                pe.wait_ge(xol, lv * 5 + 5)
                for p in range(4):
                    u = U_SIL + 8 * p
                    pe.wait_ge(kt_ready, lv * 4 + 4)
                    pe.wait_ge(ktc_ready, lv * 8 + 2 * p + 2)
                    gated(u, lambda i: chunk_update(p, i))
                    pe.wait_ge(qz_ready, lv * 8 + 2 * p + 2)
                    if p:
                        pe.wait_ge(of_ready, lv * 8 + 2 * p)
                    for a in range(2):
                        MM(heads(C[0][:, :])[:, :, a * P:(a + 1) * P], kd[:, p, a * P:(a + 1) * P], qz[:, :, a * P:(a + 1) * P],
                           start=True, stop=True, skip_group_check=True)
                    MM(heads(C[1][:, 0:2 * NS]), kd[:, p, T - P:T], qz[:, :, SEQ:T], start=True, stop=True,
                       skip_group_check=True).then_inc(sc_done, 1)
                    gated(u + 1)
                    pe.wait_ge(s_ready, lv * 4 + p + 1)
                    pe.wait_ge(st_s[p % 2], lv * 32 + 16 * (1 + p // 2))
                    pe.wait_ge(scm_ready, lv * 16 + 4 * p + 4)
                    gated(u + 2, lambda i: output(p, i))
                    pe.wait_ge(ktm_ready, lv * 4 + p + 1)
                    gated(u + 3, lambda i: sample_update(p, i))
                    if p >= 2:
                        pe.wait_ge(osb_ready, lv * 4 + 2 * (p - 2) + 2)
                        MM(C[0][:, :], cent, osb[:, PART[0]], start=True, stop=True)
                        MM(C[1][:, 0:2 * NS], cent, osb[:, PART[1]], start=True, stop=True).then_inc(xc_done, 1)
                    gated(u + 4)
                    pe.wait_ge(snew, lv * 4 + p + 1)
                    pe.wait_ge(gsq_ready, lv * 8 + 2 * p + 2)
                    MM(B[2][:, :], ones, gsq[:, PART[0]], start=True, stop=True)
                    MM(B[3][:, 0:2 * NS], ones, gsq[:, PART[1]], start=True, stop=True).then_inc(gss_done, 1)
                    gated(u + 5)
                    gated(u + 6)
                    gated(u + 7)

                BR = [A, C, B]
                pe.wait_ge(evac, lv * EVACS + 41)
                pe.wait_ge(olr, lv * 8 + 8)
                for mp in range(4):
                    for b in range(3):
                        u = U_BR + 3 * mp + b
                        if mp:
                            pe.wait_ge(br_used, lv * 24 + 6 * (mp - 1) + 2 * b + 2)
                        ready(u)
                        for mm in range(2):
                            for k in range(4):
                                xh, xl = (oh[:, 8 + k, :], ol[:, 8 + k, :]) if b == 2 else (hh[:, 4 * b + k, :], hl[:, 4 * b + k, :])
                                r = three(BR[b][mm][:, 0:T], u, (mm * 4 + k) * P, P, xh, xl, k == 0, k == 3)
                        r.then_inc(unit_done, 1)
                for m in range(KT_):
                    unit(U_OUT + m, oh, ol, T, (mgl, lv * 8) if m == 0 else None)
                    if m:
                        sumsq(m - 1, lv * 16 + 16 + m, B[3])
                sumsq(7, lv * 16 + 16 + 8, B[3])

                def ups(u0, n, j0, banks):
                    pe.sem_inc(carrier, 1)
                    with pe.Fori(0, n // 2) as i:
                        for s in range(2):
                            pe.wait_ge(f_ready, lv * FT + i * 2 + (j0 + s - 1 + 8))
                            for ab in range(2):
                                u = u0 + 2 * s + ab
                                ready(u, i * 4)
                                for k in range(KT_):
                                    r = three(banks[2 * s + ab][:, 0:T], u, k * P, P, hh[:, k, :], hl[:, k, :], k == 0, k == KT_ - 1)
                                r.then_inc(unit_done, 1)

                def downs(u0, n, j0, banks, sums):
                    u = u0
                    for q in range(2):
                        for i in range(n // 2):
                            pe.wait_ge(fl_ready, lv * FT + j0 + 2 * i + 2) if q == 0 else None
                            if q == 1 and i == 0:
                                pe.wait_ge(fl_ready, lv * FT + j0 + n)
                            ready(u)
                            for kk in range(2):
                                for mm in range(4):
                                    k = 2 * i + kk
                                    r = three(banks[q][mm][:, 0:T], u, (kk * 4 + mm) * P, P, oh[:, k, :], ol[:, k, :], k == 0, k == n - 1)
                            r.then_inc(unit_done, 1)
                            u += 1
                            if sums and q == 1 and i < 4:
                                if i == 0:
                                    pe.wait_ge(x_ready, lv * 24 + 24 + 20)
                                sumsq(i, lv * 16 + 24 + i + 1, C[1])

                pe.wait_ge(hl_ready, lv * 16 + 16)
                AC = [A[0], A[1], C[0], C[1]]
                ups(U_UP1, FA, 0, AC)
                downs(U_DN1, FA, 0, [B, AC], False)
                pe.wait_ge(x_ready, lv * 24 + 24 + 12)
                ups(U_UP2, FB, FA, B)
                pe.wait_ge(x_ready, lv * 24 + 24 + 16)
                downs(U_DN2, FB, FA, [AC, B], True)
            for m in range(4, KT_):
                sumsq(m, DEPTH * 16 + 8 + m + 1, C[1])


EVACS = 41
PER = {"act": 6, "dve": 190}


def constants():
    c = np.zeros((P, NCON), np.float64)
    r = np.arange(P)
    c[:, K_ID:K_ID + P] = np.eye(P)
    c[:, K_ONE:K_ONE + P] = 1.0
    c[:, K_CEN:K_CEN + P] = np.eye(P) - 1.0 / P
    for m in range(P):
        if m % DK < DK // 2:
            c[m + DK // 2, K_PERM + m] = -1.0
        else:
            c[m - DK // 2, K_PERM + m] = 1.0
    for a in range(2):
        c[:, K_MASK + a * P:K_MASK + (a + 1) * P] = (r[:, None] // CHUNK == r[None, :] // CHUNK) & (r[:, None] <= r[None, :])
    t = np.arange(NS)
    c[P - NS:, K_MASK + SEQ:K_MASK + T] = (t[:, None] // DEC_SEQ == t[None, :] // DEC_SEQ) & (t[:, None] <= t[None, :])
    pos = np.concatenate([np.arange(SEQ), PAST + t % DEC_SEQ])
    idx = np.concatenate([np.arange(SEQ) % CHUNK, t % DEC_SEQ])
    inv = (ROPE_BASE ** (-np.arange(DK // 2) / (DK // 2))).astype(np.float32)
    ang = (pos[None, :].astype(np.float32) * inv[r % (DK // 2)][:, None]).astype(np.float64)
    c[:, K_COS:K_COS + T] = np.cos(ang)
    c[:, K_SIN:K_SIN + T] = np.sin(ang)
    for p in range(2):
        log_g = np.log(1.0 - 2.0 ** (-5.0 - (2 * p + r // DK)))[:, None]
        c[:, K_DQ + p * T:K_DQ + (p + 1) * T] = np.exp((idx + 1)[None, :] * log_g)
        c[:, K_DK + p * T:K_DK + (p + 1) * T] = np.exp(-(idx + 1)[None, :] * log_g) * DK ** -0.5
        c[:, K_DE + 2 * p:K_DE + 2 * p + 1] = np.exp(CHUNK * log_g)
        c[:, K_DE + 2 * p + 1:K_DE + 2 * p + 2] = np.exp(DEC_SEQ * log_g)
    c[:, K_RST:K_RST + T] = idx != 0
    c[P - NS:, K_BM:K_BM + 8] = t[:, None] // DEC_SEQ == np.arange(8)[None, :]
    c[:, K_CM:K_CM + 4] = r[:, None] // CHUNK == np.arange(4)[None, :]
    return c.astype(np.float32)


def tiles(m):
    k, n = m.shape
    return m.reshape(k // P, P, n // P, P).transpose(2, 1, 0, 3).reshape(n // P, P, k)


def rows(m):
    return m.reshape(4, 2, P, 512).transpose(0, 2, 1, 3).reshape(4, P, UW)


def stream(i, a):
    w_in, w_mem, w_up, w_dn = a["w_in"][i], a["w_mem_kv"][i], a["w_up"][i], a["w_down"][i]
    sizes = [256, 256, 512, 512, 16, 256, 256, 512, 512, 512, 3 * D_MODEL]
    names = ["gq", "gk", "gv", "gr", "ga", "rq", "rk", "rv", "rg", "xq", "gates"]
    at = np.cumsum([0] + sizes)
    col = {n: w_in[:, at[j]:at[j + 1]] for j, n in enumerate(names)}
    par = np.zeros((P, UW), np.float32)
    by = lambda v: v.reshape(-1, P).T
    for o, v in ((C_N1, a["norm1_g"][i]), (C_N2, a["norm2_g"][i]), (C_MN, a["mem_norm_g"][i]), (C_BG, a["b_gate"][i]),
                 (C_CW, a["conv_w"][i]), (C_CB, a["conv_b"][i]), (C_AB, a["gla_a_b"][i]), (C_ON, a["gla_onorm_g"][i]),
                 (C_GN, a["ret_gnorm_g"][i])):
        b = by(v.reshape(-1))
        par[:, o:o + b.shape[1]] = b
    par[0:LOWRANK, C_AU:C_AU + 256] = a["gla_a_up"][i]
    par[:, C_CS:C_CS + FT * 16] = a["state_ffn_conv"][i].reshape(16, FT, P).transpose(2, 1, 0).reshape(P, FT * 16)
    ga = np.zeros((D_MODEL, P), np.float32)
    ga[:, :LOWRANK] = col["ga"]
    parts = [par[None], tiles(w_mem[:, :512]), rows(w_mem[:, 512:]), tiles(ga), tiles(col["xq"]), tiles(col["gk"]), tiles(col["gq"]),
             tiles(col["rk"]), tiles(col["rq"]), rows(col["gv"]), rows(col["rv"]), tiles(col["gr"]), tiles(col["rg"]), tiles(col["gates"])]
    br = np.stack([a[n][i] for n in ("w_br_gla", "w_br_ret", "w_br_xa")])
    br = br.reshape(3, 4, P, 4, 2, P).transpose(3, 0, 2, 4, 1, 5)
    parts += [br.reshape(12, P, UW), tiles(a["w_out"][i])]
    up = np.stack([tiles(w_up[:, :D_FF]), tiles(w_up[:, D_FF:])], 1)
    for t0, n in ((0, FA), (FA, FB)):
        dn = w_dn[t0 * P:(t0 + n) * P].reshape(n // 2, 2, P, 2, 4, P).transpose(3, 0, 2, 1, 4, 5)
        parts += [up[t0:t0 + n].reshape(2 * n, P, UW), dn.reshape(n, P, UW)]
    return np.concatenate(parts)


def pairs_of(s):
    d, b = s.shape[:2]
    return s.reshape(d, b, 2, P, DV).transpose(0, 2, 3, 1, 4)


def kernel(**inputs):
    import concourse.bacc as bacc
    from concourse.bass_utils import run_bass_kernel_spmd

    a = {k: np.asarray(v) for k, v in inputs.items()}
    fm = lambda m: m.reshape(-1, KT_, P).transpose(2, 1, 0)
    data = {
        "w": np.concatenate([stream(i, a) for i in range(DEPTH)]),
        "x_in": np.concatenate([fm(a["x_prompt"]), fm(a["x_sample"])], 2),
        "mem_in": fm(a["mem_prompt"]),
        "cache_k": a["cache_mem_k"].transpose(0, 1, 4, 3, 2).reshape(DEPTH, DEC_BATCH, P, 1024),
        "cache_v": a["cache_mem_v"].reshape(DEPTH, DEC_BATCH, 2, P, 512).transpose(0, 1, 3, 2, 4).reshape(DEPTH, DEC_BATCH, P, 1024),
        "st_in": np.concatenate([pairs_of(a["state_gla"]), pairs_of(a["state_ret"])], 1),
        "consts": constants(),
        "final_g": a["final_g"].reshape(KT_, P).T,
    }
    data = {k: np.ascontiguousarray(v) for k, v in data.items()}
    outs = {"y_out": (P, KT_, T), "pst_out": (DEPTH, 4, P, P), "sst_out": (DEPTH, 4, P, DEC_BATCH, P),
            "conv_out": (DEPTH, P, FT, 18), "mk_out": (DEPTH, P, 4, MEM), "mv_out": (DEPTH, P, 2, 512)}
    nc = bacc.Bacc("TRN2", target_bir_lowering=False, num_devices=1, dynamic_dma_scratch_size=1024)
    args = [nc.dram_tensor(k, v.shape, mybir.dt.float32, kind="ExternalInput").ap() for k, v in data.items()]
    args += [nc.dram_tensor(k, s, mybir.dt.float32, kind="ExternalOutput").ap() for k, s in outs.items()]
    build_trunk(nc, *args)
    r = run_bass_kernel_spmd(nc, [data], core_ids=[0]).results[0]

    y = r["y_out"].transpose(2, 1, 0).reshape(T, D_MODEL)
    pst = r["pst_out"].reshape(DEPTH, 2, HEADS, DK, DV)
    sst = r["sst_out"].reshape(DEPTH, 2, 2, P, DEC_BATCH, DV).transpose(1, 0, 4, 2, 3, 5).reshape(2, DEPTH, DEC_BATCH, HEADS, DK, DV)
    conv = r["conv_out"].transpose(0, 3, 2, 1).reshape(DEPTH, 18, D_FF)
    mk = r["mk_out"].transpose(0, 3, 2, 1)
    mv = r["mv_out"].transpose(0, 2, 1, 3).reshape(DEPTH, MEM, HEADS, DV)
    c = np.ascontiguousarray
    return (c(y[:SEQ].reshape(1, SEQ, D_MODEL)), c(y[SEQ:].reshape(DEC_BATCH, DEC_SEQ, D_MODEL)),
            c(pst[:, 0][:, None]), c(pst[:, 1][:, None]), c(conv[:, :2][:, None]), c(mk[:, None]), c(mv[:, None]),
            c(sst[0]), c(sst[1]), c(conv[:, 2:].reshape(DEPTH, DEC_BATCH, 2, D_FF)))
```
